# Optimizing a Trainium2 kernel written in Bass

```python
import jax, jax.numpy as jnp
from jax import lax
import numpy as np

D_MODEL = 1024
BATCH = 1
SEQ = 256
DEPTH = 4
DEC_BATCH = 8
DEC_SEQ = 1
PAST_LEN = 256
PAGE_SIZE = 128

N_MIXERS = 3
N_RET_LAYERS = (DEPTH + 2) // 3
N_POOL_LAYERS = (DEPTH + 1) // 3
N_ATT_LAYERS = DEPTH // 3

RET_HEADS = 4
RET_DK = D_MODEL // RET_HEADS
RET_DV = 2 * D_MODEL // RET_HEADS
RET_CHUNK = 128
RET_IN = 2 * RET_HEADS * RET_DK + 2 * RET_HEADS * RET_DV

POOL_WINDOWS = (2, 4, 8, 16)
POOL_GROUPS = len(POOL_WINDOWS)
POOL_GW = D_MODEL // POOL_GROUPS
POOL_PREV = max(POOL_WINDOWS) - 1

ATT_GROUPS = ((128, 1), (512, 4), (2048, 16))
ATT_HEADS = 16
ATT_DH = D_MODEL // ATT_HEADS
ATT_IN = len(ATT_GROUPS) * 3 * ATT_HEADS * ATT_DH

FFN_HIDDEN = ((8 * D_MODEL + 3 * 256 - 1) // (3 * 256)) * 256

NORM_EPS = 1e-6
GN_EPS = 1e-5
NEG_INF = -1e30

kernel_name = 'hybrid_retention_pool_dilated_decoder_step'

def rms_norm(x, g):
    xf = x.astype(jnp.float32)
    y = xf * lax.rsqrt(jnp.mean(xf * xf, axis=-1, keepdims=True) + NORM_EPS)
    return (y * g.astype(jnp.float32)).astype(x.dtype)

def swiglu(xn, w_in, w_out):
    gate, up = jnp.split(xn @ w_in, 2, axis=-1)
    return (jax.nn.silu(gate) * up) @ w_out

def ret_log_gamma():
    return jnp.log1p(-jnp.exp2(-5.0 - jnp.arange(RET_HEADS, dtype=jnp.float32)))

def alibi_slopes():
    n = len(ATT_GROUPS) * ATT_HEADS
    s = jnp.exp2(-8.0 * jnp.arange(1, n + 1, dtype=jnp.float32) / n)
    return s.reshape(len(ATT_GROUPS), ATT_HEADS)

def retention_scan(q, k, v, s0):
    B, L, H, _ = q.shape
    c = RET_CHUNK if L % RET_CHUNK == 0 else L
    nc = L // c
    lg = ret_log_gamma()
    n = jnp.arange(c, dtype=jnp.float32)
    diff = n[:, None] - n[None, :]
    decay = jnp.where(diff[None] >= 0,
                      jnp.exp(jnp.maximum(diff, 0.0)[None] * lg[:, None, None]), 0.0)
    xi = jnp.exp((n[:, None] + 1.0) * lg[None, :])
    zeta = jnp.exp((c - 1.0 - n)[:, None] * lg[None, :])
    g_c = jnp.exp(c * lg)

    def chunks(t):
        return t.astype(jnp.float32).reshape(B, nc, c, H, t.shape[-1]).transpose(1, 0, 2, 3, 4)

    def step(s, inp):
        qc, kc, vc = inp
        a = jnp.einsum('bnhk,bmhk->bhnm', qc, kc) * decay
        o = (jnp.einsum('bhnm,bmhv->bnhv', a, vc)
             + jnp.einsum('bnhk,bhkv->bnhv', qc, s) * xi[None, :, :, None])
        s = g_c[None, :, None, None] * s + jnp.einsum('bmhk,bmhv->bhkv', kc * zeta[None, :, :, None], vc)
        return s, o

    s, o = lax.scan(step, s0.astype(jnp.float32), (chunks(q), chunks(k), chunks(v)))
    o = o.transpose(1, 0, 2, 3, 4).reshape(B, L, H, RET_DV)
    return o, s

def retention_mixer(xn, s0, w_in, w_out):
    B, L, _ = xn.shape
    hk, hv = RET_HEADS * RET_DK, RET_HEADS * RET_DV
    q, k, v, g = jnp.split(xn @ w_in, [hk, 2 * hk, 2 * hk + hv], axis=-1)
    q = q.reshape(B, L, RET_HEADS, RET_DK) * (RET_DK ** -0.5)
    k = k.reshape(B, L, RET_HEADS, RET_DK)
    v = v.reshape(B, L, RET_HEADS, RET_DV)
    o, s = retention_scan(q, k, v, s0)
    mu = jnp.mean(o, axis=-1, keepdims=True)
    var = jnp.mean(jnp.square(o - mu), axis=-1, keepdims=True)
    o = (o - mu) * lax.rsqrt(var + GN_EPS)
    o = o.reshape(B, L, hv) * jax.nn.silu(g.astype(jnp.float32))
    return o.astype(xn.dtype) @ w_out, s

def pool_mixer(xn, prev, pos0, w_grp, scale):
    B, L, _ = xn.shape
    P = POOL_PREV
    xp = jnp.concatenate([prev.astype(jnp.float32), xn.astype(jnp.float32)], axis=1)
    cs = jnp.concatenate([jnp.zeros((B, 1, D_MODEL), jnp.float32), jnp.cumsum(xp, axis=1)], axis=1)
    pos = pos0 + jnp.arange(L)
    outs = []
    for gi, w in enumerate(POOL_WINDOWS):
        sl = slice(gi * POOL_GW, (gi + 1) * POOL_GW)
        wsum = cs[:, P + 1:P + 1 + L, sl] - cs[:, P + 1 - w:P + 1 - w + L, sl]
        cnt = jnp.minimum(pos + 1, w).astype(jnp.float32)
        outs.append(wsum / cnt[None, :, None] - xp[:, P:, sl])
    z = jnp.stack(outs, axis=2)
    y = jnp.einsum('blgc,gcd->blgd', z, w_grp.astype(jnp.float32)).reshape(B, L, D_MODEL)
    y = y * scale.astype(jnp.float32)
    return y.astype(xn.dtype), xp[:, -P:].astype(xn.dtype)

def dilated_band_prompt(q, k, v, dil, n_keys, slopes):
    B, S, H, Dh = q.shape
    Ls = S // dil
    b = n_keys
    nb = -(-Ls // b)
    Lp = nb * b

    def split(t):
        return t.reshape(B, Ls, dil, H, Dh).transpose(0, 2, 1, 3, 4)

    qb = jnp.pad(split(q), ((0, 0), (0, 0), (0, Lp - Ls), (0, 0), (0, 0))).reshape(B, dil, nb, b, H, Dh)

    def band(t):
        tp = jnp.pad(split(t), ((0, 0), (0, 0), (b, Lp - Ls), (0, 0), (0, 0)))
        prv = tp[:, :, :Lp].reshape(B, dil, nb, b, H, Dh)
        cur = tp[:, :, b:].reshape(B, dil, nb, b, H, Dh)
        return jnp.concatenate([prv, cur], axis=3)

    kb, vb = band(k), band(v)
    qi = jnp.arange(b)[:, None]
    j = jnp.arange(2 * b)[None, :]
    dist = qi + b - j
    blk = jnp.arange(nb)[:, None, None]
    mask = (dist >= 0) & (dist <= n_keys) & (blk * b - b + j >= 0)
    bias = -slopes[:, None, None] * (dil * dist).astype(jnp.float32)
    s = jnp.einsum('brnqhe,brnkhe->brnhqk', qb, kb) * (ATT_DH ** -0.5) + bias
    s = jnp.where(mask[:, None], s, NEG_INF)
    m = jnp.max(s, axis=-1)
    p = jnp.exp(s - m[..., None])
    l = jnp.sum(p, axis=-1)
    o = jnp.einsum('brnhqk,brnkhe->brnqhe', p, vb) / jnp.swapaxes(l, -1, -2)[..., None]

    def merge(t):
        tail = t.shape[4:]
        t = t.reshape((B, dil, Lp) + tail)[:, :, :Ls]
        return jnp.swapaxes(t, 1, 2).reshape((B, S) + tail)

    return merge(o), merge(jnp.swapaxes(m, -1, -2)), merge(jnp.swapaxes(l, -1, -2))

def dilated_gather_decode(q, kv_new, kv_cache, dil, n_keys, slopes):
    Wb = kv_cache.shape[1]
    T = q.shape[1]
    kk = jnp.arange(n_keys + 1)
    idx = Wb + jnp.arange(T)[:, None] - dil * kk[None, :]
    from_cache = kv_cache[:, jnp.clip(idx, 0, Wb - 1)]
    from_new = kv_new[:, jnp.clip(idx - Wb, 0, T - 1)]
    kvg = jnp.where((idx < Wb)[None, :, :, None, None, None], from_cache, from_new).astype(jnp.float32)
    s = (jnp.einsum('bthe,btkhe->bthk', q, kvg[:, :, :, 0]) * (ATT_DH ** -0.5)
         - slopes[:, None] * (dil * kk).astype(jnp.float32)[None, :])
    s = jnp.where((idx >= 0)[None, :, None, :], s, NEG_INF)
    m = jnp.max(s, axis=-1)
    p = jnp.exp(s - m[..., None])
    l = jnp.sum(p, axis=-1)
    o = jnp.einsum('bthk,btkhe->bthe', p, kvg[:, :, :, 1]) / l[..., None]
    return o, m, l

def attn_mixer(xn, kv_caches, w_in, w_out):
    B, L, _ = xn.shape
    G = len(ATT_GROUPS)
    proj = (xn @ w_in).reshape(B, L, G, 3, ATT_HEADS, ATT_DH)
    slopes = alibi_slopes()
    outs, ms, ls, new_kv = [], [], [], []
    for gi, (w, d) in enumerate(ATT_GROUPS):
        q = proj[:, :, gi, 0].astype(jnp.float32)
        kv = proj[:, :, gi, 1:]
        if kv_caches is None:
            o, m, l = dilated_band_prompt(q, kv[:, :, 0].astype(jnp.float32),
                                          kv[:, :, 1].astype(jnp.float32), d, w // d, slopes[gi])
            new_kv.append(kv[:, -min(w, L):])
        else:
            o, m, l = dilated_gather_decode(q, kv, kv_caches[gi], d, w // d, slopes[gi])
            new_kv.append(kv)
        outs.append(o)
        ms.append(m)
        ls.append(l)
    m_all = jnp.stack(ms)
    wts = jnp.stack(ls) * jnp.exp(m_all - jnp.max(m_all, axis=0))
    o = jnp.einsum('gblh,gblhe->blhe', wts, jnp.stack(outs)) / jnp.sum(wts, axis=0)[..., None]
    return o.reshape(B, L, D_MODEL).astype(xn.dtype) @ w_out, new_kv

def setup_inputs(seed: int = 0) -> dict:
    key = jax.random.key(seed)
    ks = jax.random.split(key, 16)
    d = D_MODEL

    def nrm(k, shape, scale=1.0):
        return jax.random.normal(k, shape, jnp.float32) * scale

    wb = [min(w, PAST_LEN) for (w, _) in ATT_GROUPS]
    return {
        'x_prompt': nrm(ks[0], (BATCH, SEQ, d)),
        'x_sample': nrm(ks[1], (DEC_BATCH, DEC_SEQ, d)),
        'state_ret': nrm(ks[2], (N_RET_LAYERS, DEC_BATCH, RET_HEADS, RET_DK, RET_DV)),
        'state_pool': nrm(ks[3], (N_POOL_LAYERS, DEC_BATCH, POOL_PREV, d)),
        'cache_kv_g0': nrm(ks[4], (N_ATT_LAYERS, DEC_BATCH, wb[0], 2, ATT_HEADS, ATT_DH)),
        'cache_kv_g1': nrm(ks[5], (N_ATT_LAYERS, DEC_BATCH, wb[1], 2, ATT_HEADS, ATT_DH)),
        'cache_kv_g2': nrm(ks[6], (N_ATT_LAYERS, DEC_BATCH, wb[2], 2, ATT_HEADS, ATT_DH)),
        'norm_gains': 1.0 + nrm(ks[7], (DEPTH, 4, d), 0.05),
        'w_in_ret': nrm(ks[8], (N_RET_LAYERS, d, RET_IN), d ** -0.5),
        'w_out_ret': nrm(ks[9], (N_RET_LAYERS, RET_HEADS * RET_DV, d), (RET_HEADS * RET_DV) ** -0.5),
        'w_grp_pool': nrm(ks[10], (N_POOL_LAYERS, POOL_GROUPS, POOL_GW, POOL_GW), POOL_GW ** -0.5),
        'scale_pool': 1.0 + nrm(ks[11], (N_POOL_LAYERS, d), 0.1),
        'w_in_attn': nrm(ks[12], (N_ATT_LAYERS, d, ATT_IN), d ** -0.5),
        'w_out_attn': nrm(ks[13], (N_ATT_LAYERS, d, d), d ** -0.5),
        'w_ffn_in': nrm(ks[14], (DEPTH, d, 2 * FFN_HIDDEN), d ** -0.5),
        'w_ffn_out': nrm(ks[15], (DEPTH, FFN_HIDDEN, d), FFN_HIDDEN ** -0.5),
    }

def reference(x_prompt, x_sample, state_ret, state_pool, cache_kv_g0, cache_kv_g1, cache_kv_g2,
              norm_gains, w_in_ret, w_out_ret, w_grp_pool, scale_pool,
              w_in_attn, w_out_attn, w_ffn_in, w_ffn_out):
    B = x_prompt.shape[0]
    caches = (cache_kv_g0, cache_kv_g1, cache_kv_g2)
    xp, xs = x_prompt, x_sample
    ret_p, ret_s, pool_p, pool_s = [], [], [], []
    kv_p = [[] for _ in ATT_GROUPS]
    kv_s = [[] for _ in ATT_GROUPS]
    for i in range(DEPTH):
        kind, j = i % N_MIXERS, i // N_MIXERS
        g = norm_gains[i]
        hp, hs = rms_norm(xp, g[0]), rms_norm(xs, g[0])
        if kind == 0:
            s0 = jnp.zeros((B, RET_HEADS, RET_DK, RET_DV), jnp.float32)
            mp, sp = retention_mixer(hp, s0, w_in_ret[j], w_out_ret[j])
            ms, ss = retention_mixer(hs, state_ret[j], w_in_ret[j], w_out_ret[j])
            ret_p.append(sp)
            ret_s.append(ss)
        elif kind == 1:
            prev0 = jnp.zeros((B, POOL_PREV, D_MODEL), hp.dtype)
            mp, sp = pool_mixer(hp, prev0, 0, w_grp_pool[j], scale_pool[j])
            ms, ss = pool_mixer(hs, state_pool[j], PAST_LEN, w_grp_pool[j], scale_pool[j])
            pool_p.append(sp)
            pool_s.append(ss)
        else:
            mp, kvp = attn_mixer(hp, None, w_in_attn[j], w_out_attn[j])
            ms, kvs = attn_mixer(hs, [c[j] for c in caches], w_in_attn[j], w_out_attn[j])
            for gi in range(len(ATT_GROUPS)):
                kv_p[gi].append(kvp[gi])
                kv_s[gi].append(kvs[gi])
        xp = xp + rms_norm(mp, g[1])
        xs = xs + rms_norm(ms, g[1])
        xp = xp + rms_norm(swiglu(rms_norm(xp, g[2]), w_ffn_in[i], w_ffn_out[i]), g[3])
        xs = xs + rms_norm(swiglu(rms_norm(xs, g[2]), w_ffn_in[i], w_ffn_out[i]), g[3])
    return (xp, xs,
            jnp.stack(ret_p), jnp.stack(ret_s),
            jnp.stack(pool_p), jnp.stack(pool_s),
            jnp.stack(kv_p[0]), jnp.stack(kv_s[0]),
            jnp.stack(kv_p[1]), jnp.stack(kv_s[1]),
            jnp.stack(kv_p[2]), jnp.stack(kv_s[2]))


_drawn_inputs = setup_inputs


def setup_inputs(seed=0):
    import zlib

    import numpy as np

    out = dict(_drawn_inputs(seed))
    spreads = {}
    factors = {}
    for name, (base, spread) in spreads.items():
        noise = np.random.default_rng([zlib.crc32(name.encode()), seed]).standard_normal(out[name].shape)
        drawn = base * np.exp(spread * noise) if base else spread * noise
        out[name] = __import__('jax').numpy.asarray(drawn.astype(out[name].dtype))
    for name, factor in factors.items():
        out[name] = (out[name] * factor).astype(out[name].dtype)
    return out
```

```python
from contextlib import ExitStack

import numpy as np
import concourse.bass as bass
from concourse import mybir

F32 = mybir.dt.float32
F32R = mybir.dt.float32r
ALU = mybir.AluOpType
ACT = mybir.ActivationFunctionType
AX = mybir.AxisListType

P = 128
D = 1024
SEQ = 256
DECB = 8
T = SEQ + DECB
KD = D // P
DEPTH = 4
FFN = 2816
KF = FFN // P
RH, RDK, RDV = 4, 256, 512
AH, ADH = 16, 64
GROUPS = ((128, 1), (512, 4), (2048, 16))
WINDOWS = (2, 4, 8, 16)
PREV = 15
EPS_RMS, EPS_GN = 1e-6, 1e-5
GAMMA = [1.0 - 2.0 ** (-5 - h) for h in range(RH)]

UC = 256
UMAX = 8 * UC
RAW = 4
SPL = 2
FO_K = ((0, 6), (6, 11), (11, 17), (17, 22))

N_SUB = 2 * DEPTH


def slopes():
    n = len(GROUPS) * AH
    return (2.0 ** (-8.0 * np.arange(1, n + 1) / n)).reshape(len(GROUPS), AH)


def shape_tables():
    base = np.zeros((P, 2 * P + 2), np.float32)
    base[:, 0:P] = np.eye(P)
    base[:, P:2 * P] = 1.0
    base[:, 2 * P] = EPS_RMS
    base[:, 2 * P + 1] = EPS_GN

    lg = np.log1p(-np.exp2(-5.0 - np.arange(RH)))
    n = np.arange(P)
    ret = np.zeros((P, RET_TAB), np.float32)
    for h in range(RH):
        d = n[None, :] - n[:, None]
        ret[:, h * P:(h + 1) * P] = np.where(d >= 0, np.exp(np.maximum(d, 0) * lg[h]), 0.0) / 16.0
        ret[:, (RH + h) * P:(RH + h + 1) * P] = (np.exp((n + 1.0) * lg[h]) / 16.0)[None, :]
        ret[:, 2 * RH * P + h] = np.exp((P - 1.0 - n) * lg[h])
    for b in range(DECB):
        ret[:, 2 * RH * P + RH + b] = (n % 32 == b)

    pool = np.zeros((P, 4 * T), np.float32)
    for g, w in enumerate(WINDOWS):
        cnt = np.full(T, float(w))
        cnt[0:SEQ] = np.minimum(np.arange(SEQ) + 1, w)
        pool[:, g * T:(g + 1) * T] = 1.0 / cnt

    s = slopes()
    att = np.zeros((P, ATT_TAB), np.float32)
    at = 0
    for c in range(2):
        for g, (w, dil) in enumerate(GROUPS):
            q = (c * P + n)[:, None]
            j = np.arange((c + 1) * P)[None, :]
            dist = q - j
            ok = (dist >= 0) & (dist % dil == 0) & (dist // dil <= w // dil)
            att[:, at:at + (c + 1) * P] = np.where(ok, dist * (s[g, 0] / s[0, 0]), 1e32)
            at += (c + 1) * P
    for h in range(AH):
        att[:, at + h] = -s[0, h] * (P - n)
    b_new = np.full((P, AH), -1e30)
    for h in range(AH):
        b_new[0:64, h] = -s[1, h] * 4.0 * (64 - n[0:64])
        b_new[64:80, h] = -s[2, h] * 16.0 * (16 - n[0:16])
        b_new[96:99, h] = 0.0
    att[:, at + AH:at + 2 * AH] = b_new
    return base, ret, pool, att


RET_TAB = 2 * RH * P + RH + DECB
ATT_TAB = 3 * P + 6 * P + 2 * AH


def trunk(nc, io):
    (x_prompt, x_sample, state_ret, state_pool, cache0, cache1, cache2, gains_d, w_in_ret, w_out_ret,
     w_grp, scale_pool, w_in_attn, w_out_attn, w_ffn_in, w_ffn_out, t_base, t_ret, t_pool, t_att,
     y_prompt, y_sample, ret_p, ret_s, pool_p, pool_s, kv0_p, kv0_s, kv1_p, kv1_s, kv2_p, kv2_s) = io
    caches, kv_p, kv_s = (cache0, cache1, cache2), (kv0_p, kv1_p, kv2_p), (kv0_s, kv1_s, kv2_s)

    def rows(w):
        return w.rearrange("(k p) n -> p k n", p=P)

    units = []
    where = {}

    for sub in range(N_SUB):
        lay = sub // 2
        where[sub, "in"] = len(units)
        if sub % 2:
            wi, wo = rows(w_ffn_in[lay]), rows(w_ffn_out[lay])
            for pr in range(KF // 2):
                units.append(wi[:, :, pr * UC:(pr + 1) * UC])
                units.append(wi[:, :, FFN + pr * UC:FFN + (pr + 1) * UC])
            where[sub, "out"] = len(units)
            for p in range(4):
                for a, b in FO_K:
                    units.append(wo[:, a:b, p * UC:(p + 1) * UC])
        elif lay % 3 == 0:
            wi, wo = rows(w_in_ret[lay // 3]), rows(w_out_ret[lay // 3])
            for h in range(RH):
                for c in (h * RDK, D + h * RDK, 2 * D + h * RDV, 2 * D + h * RDV + UC,
                          4 * D + h * RDV, 4 * D + h * RDV + UC):
                    units.append(wi[:, :, c:c + UC])
            where[sub, "out"] = len(units)
            for p, a in ((0, 0), (1, 0), (0, 8), (1, 8), (2, 0), (2, 8), (3, 0), (3, 8)):
                units.append(wo[:, a:a + 8, p * UC:(p + 1) * UC])
        elif lay % 3 == 1:
            where[sub, "out"] = len(units)
            for g in range(4):
                units.append(rows(w_grp[0, g]))
        else:
            wi, wo = rows(w_in_attn[0]), rows(w_out_attn[0])
            for quad in range(4):
                for g in range(3):
                    for kind in range(3):
                        c = (g * 3 + kind) * D + quad * UC
                        units.append(wi[:, :, c:c + UC])
            where[sub, "out"] = len(units)
            for p in range(4):
                units.append(wo[:, :, p * UC:(p + 1) * UC])
    NU = len(units)
    size = [int(np.prod(u.shape[1:])) for u in units]
    pair_at = {}
    npair = 0
    for sub in range(N_SUB):
        pair_at[sub, "in"] = npair
        if sub % 2:
            npair += KF
        elif sub // 2 % 3 == 0:
            npair += 24
        elif sub // 2 % 3 == 2:
            npair += 36
        pair_at[sub, "out"] = npair
        npair += 4
    ret_subs = [s for s in range(0, N_SUB, 2) if s // 2 % 3 == 0]
    POOL_SUB, ATT_SUB = 2, 4

    def gbase(sub):
        return KD * (sub - (1 if sub > POOL_SUB else 0))

    ctx = ExitStack()
    with ctx:
        def sb(name, shape, dt=F32, stack=ctx):
            return stack.enter_context(nc.sbuf_tensor(name, shape, dt))

        def sem(name):
            return ctx.enter_context(nc.semaphore(name))

        acc = ctx.enter_context(nc.psum_tensor("acc", [P, 4, 512], F32))
        mix = ctx.enter_context(nc.psum_tensor("mix", [P, 4, 512], F32))

        raw = sb("raw", [P, RAW, UMAX])
        w_hi = sb("w_hi", [P, SPL, UMAX], F32R)
        w_lo = sb("w_lo", [P, SPL, UMAX], F32R)
        xT = sb("xT", [P, KD, T])
        y = sb("y", [P, KD, T])
        sq = sb("sq", [P, KD, T])
        g_hi = sb("g_hi", [P, KD, T], F32R)
        g_lo = sb("g_lo", [P, KD, T], F32R)
        tbase = sb("tbase", [P, 2 * P + 2])
        gains = sb("gains", [P, KD, 17])
        std = sb("std", [P, T])
        rstd_post = sb("rstd_post", [P, T])
        rstd_pre = sb("rstd_pre", [P, T])
        ident, ones = tbase[:, 0:P], tbase[:, P:2 * P]
        eps_rms, eps_gn = tbase[:, 2 * P:2 * P + 1], tbase[:, 2 * P + 1:2 * P + 2]

        with ExitStack() as s:
            h_hi = sb("h_hi", [P, KF, T], F32R, s)
            h_lo = sb("h_lo", [P, KF, T], F32R, s)
            gate = sb("gate", [P, 2, 2, T], F32, s)
            silu_gate = sb("silu_gate", [P, 2, 2, T], F32, s)
            up = sb("up", [P, 2, T], F32, s)
            hid = sb("hid", [P, 2, 2, T], F32, s)
        with ExitStack() as s:
            ro_hi = sb("ro_hi", [P, 16, T], F32R, s)
            ro_lo = sb("ro_lo", [P, 16, T], F32R, s)
            tret = sb("tret", [P, RET_TAB], F32, s)
            rq = sb("rq", [P, 2, 2, T], F32, s)
            rk = sb("rk", [P, 2, T], F32, s)
            rv = sb("rv", [P, 2, 2, T], F32, s)
            vrow = sb("vrow", [P, 2, RDV], F32, s)
            kz = sb("kz", [P, 2, RDK], F32, s)
            scoresT = sb("scoresT", [P, 2, P], F32, s)
            q_xi = sb("q_xi", [P, 2, P], F32, s)
            S0 = sb("S0", [P, 2, RDV], F32, s)
            k_row = sb("k_row", [DECB, RDK], F32, s)
            v_row = sb("v_row", [DECB, RDV], F32, s)
            k_stack = sb("k_stack", [P, RDK], F32R, s)
            v_stack = sb("v_stack", [P, RDV], F32R, s)
            k_one = sb("k_one", [P, 2, RDK], F32R, s)
            gsq = sb("gsq", [P, 4, T], F32, s)
            gstd = sb("gstd", [P, T], F32, s)
            grstd = sb("grstd", [P, T], F32, s)
            st_in = sb("st_in", [P, 3, 2, RDV], F32, s)
            st_out = sb("st_out", [P, 2, 2, RDV], F32, s)
        with ExitStack() as s:
            tpool = sb("tpool", [P, 4, T], F32, s)
            xn = sb("xn", [P, KD, T], F32, s)
            pad = sb("pad", [P, 2, 2, 16 + SEQ], F32, s)
            wsum = sb("wsum", [P, 2, T], F32, s)
            zf = sb("zf", [P, 2, 2, T], F32, s)
            prev = sb("prev", [DECB * PREV, D], F32, s)
            prevT = sb("prevT", [P, KD, DECB * PREV], F32, s)
            pout = sb("pout", [16, 2, D], F32, s)
        with ExitStack() as s:
            tatt = sb("tatt", [P, ATT_TAB], F32, s)
            aq = sb("aq", [P, 2, 3, 2, T], F32, s)
            ak = sb("ak", [P, 2, 3, 2, T], F32, s)
            avrow = sb("avrow", [P, 2, 3, 2, UC], F32, s)
            srow = sb("srow", [DECB, 2, 3, 2, UC], F32, s)
            sc = sb("sc", [P, 2, 6 * P], F32, s)
            pT = sb("pT", [P, 6 * P], F32, s)
            nmax = sb("nmax", [P, 2], F32, s)
            lsum = sb("lsum", [P, 2], F32, s)
            rl = sb("rl", [P, 2], F32, s)
            kc = sb("kc", [P, DECB, 2, UC], F32, s)
            vc = sb("vc", [P, DECB, 2, UC], F32, s)
            dprod = sb("dprod", [P, 2, UC], F32, s)
            dS = sb("dS", [P, 2, DECB, 4], F32, s)
            dP = sb("dP", [32, 227], F32, s)
            dPT = sb("dPT", [P, 2, 32], F32, s)
            dst = sb("dst", [32, 4], F32, s)
        with ExitStack() as s:
            rows_out = sb("rows_out", [P, 2, D], F32, s)
            srows_out = sb("srows_out", [DECB, D], F32, s)

        DT = tret[:, 0:RH * P].rearrange("p (h n) -> p h n", h=RH)
        XI = tret[:, RH * P:2 * RH * P].rearrange("p (h n) -> p h n", h=RH)
        zeta = tret[:, 2 * RH * P:2 * RH * P + RH]
        one_b = tret[:, 2 * RH * P + RH:RET_TAB]
        oT = y[:, :, :].rearrange("p (r v) t -> p r v t", r=2)
        gT = sq[:, :, :].rearrange("p (r v) t -> p r v t", r=2)
        av = sq[:, 0:2, :]
        akrow = sq[:, 4:6, 0:UC]
        TB = (tatt[:, 0:3 * P], tatt[:, 3 * P:9 * P])
        dbias = tatt[:, 9 * P:9 * P + 2 * AH].rearrange("p (x h) -> p x h", x=2)

        in_x, in_tab = sem("in_x"), sem("in_tab")
        raw_landed = [sem(f"raw_landed{i}") for i in range(RAW)]
        hi_split, lo_even, lo_odd = sem("hi_split"), sem("lo_even"), sem("lo_odd")
        unit_done, acc_read = sem("unit_done"), sem("acc_read")
        init_turned, init_read = sem("init_turned"), sem("init_read")
        dve_step = sem("dve_step")
        y_squared, y_gained, post_summed = sem("y_squared"), sem("y_gained"), sem("post_summed")
        ao_hi_ready, ao_lo_ready = sem("ao_hi_ready"), sem("ao_lo_ready")
        stat, std_ready, rstd_ready = sem("stat"), sem("std_ready"), sem("rstd_ready")
        x_new, g_hi_ready, g_lo_ready = sem("x_new"), sem("g_hi_ready"), sem("g_lo_ready")
        x_squared, pre_summed = sem("x_squared"), sem("pre_summed")
        silu_done, hid_ready = sem("silu_done"), sem("hid_ready")
        h_hi_ready, h_lo_ready = sem("h_hi_ready"), sem("h_lo_ready")
        tab_ret, stack_zeroed = sem("tab_ret"), sem("stack_zeroed")
        st_landed = [sem(f"st_landed{i}") for i in range(3)]
        st_stored = [sem(f"st_stored{i}") for i in range(2)]
        k_one_ready, outer_done, st_updated, qs_done, os_ready = (
            sem("k_one_ready"), sem("outer_done"), sem("st_updated"), sem("qs_done"), sem("os_ready"))
        a_done, at_ready, tk_done, krow_ready, kz_ready = (
            sem("a_done"), sem("at_ready"), sem("tk_done"), sem("krow_ready"), sem("kz_ready"))
        tv_done, vrow_ready, k_stack_hi, k_stack_ready, v_stack_hi, v_stack_ready = (
            sem("tv_done"), sem("vrow_ready"), sem("k_stack_hi"), sem("k_stack_ready"),
            sem("v_stack_hi"), sem("v_stack_ready"))
        s0_done, s0_ready, o_done, o_ready, s1_done, s1_ready, s1_stored = (
            sem("s0_done"), sem("s0_ready"), sem("o_done"), sem("o_ready"), sem("s1_done"),
            sem("s1_ready"), sem("s1_stored"))
        g_silu = sem("g_silu")
        gn_sum, gn_mu, gn_cent, gn_sq, gn_sum2, gn_var, gn_std, gn_out = (
            sem("gn_sum"), sem("gn_mu"), sem("gn_cent"), sem("gn_sq"), sem("gn_sum2"), sem("gn_var"),
            sem("gn_std"), sem("gn_out"))
        ro_hi_ready, ro_lo_ready = sem("ro_hi_ready"), sem("ro_lo_ready")
        tab_pool, prev_in, pool_copied = sem("tab_pool"), sem("prev_in"), sem("pool_copied")
        prev_turned, prevT_ready, xn_ready, xn_turned, pout_ready, pool_stored = (
            sem("prev_turned"), sem("prevT_ready"), sem("xn_ready"), sem("xn_turned"), sem("pout_ready"),
            sem("pool_stored"))
        z_ready, z_hi_ready, z_lo_ready, pad_zeroed = (
            sem("z_ready"), sem("z_hi_ready"), sem("z_lo_ready"), sem("pad_zeroed"))
        tab_att, cache_zeroed, cache_in = sem("tab_att"), sem("cache_zeroed"), sem("cache_in")
        row_turned, row_evac, kv_stored = sem("row_turned"), sem("row_evac"), sem("kv_stored")
        new_in = [sem(f"new_in{i}") for i in range(2)]
        row_stored = [sem(f"row_stored{i}") for i in range(2)]
        srow_stored = [sem(f"srow_stored{i}") for i in range(2)]
        sc_done, sc_biased, max_ready, p_exp, rl_ready, p_ready = (
            sem("sc_done"), sem("sc_biased"), sem("max_ready"), sem("p_exp"), sem("rl_ready"), sem("p_ready"))
        pt_done, pt_ready, pv_done, pv_read = sem("pt_done"), sem("pt_ready"), sem("pv_done"), sem("pv_read")
        qb_done, qb_read, ds_ready, ds_turned, dmax_ready, dp_exp, dp_ready, dpt_done, dpt_ready, dpv_done, \
            dpv_read = (sem("qb_done"), sem("qb_read"), sem("ds_ready"), sem("ds_turned"), sem("dmax_ready"),
                        sem("dp_exp"), sem("dp_ready"), sem("dpt_done"), sem("dpt_ready"), sem("dpv_done"),
                        sem("dpv_read"))
        fin_turned, fin_ready, stored = sem("fin_turned"), sem("fin_ready"), sem("stored")

        block = ctx.enter_context(nc.Block())

        @block.sync
        def _(sp):
            def send(u, src):
                k = src.shape[1]
                sp.dma_start(raw[:, u % RAW, 0:k * UC].rearrange("p (k n) -> p k n", k=k), src)\
                    .then_inc(raw_landed[u % RAW], 16)

            def load(u, src, i=None):
                if u >= RAW:
                    n = (u - RAW) // 2 + 1
                    sp.wait_ge(lo_even if u % 2 == 0 else lo_odd, n if i is None else i * 2 + n)
                send(u, src)

            for sub in range(N_SUB):
                u0 = where[sub, "in"]
                end = where[sub + 1, "in"] if sub + 1 < N_SUB else NU
                if sub % 2 == 0:
                    for u in range(u0, end):
                        load(u, units[u])
                    continue
                wi, wo = rows(w_ffn_in[sub // 2]), rows(w_ffn_out[sub // 2])
                with sp.Fori(0, 5) as i:
                    for j in range(4):
                        load(u0 + j, wi[:, :, bass.ds(i * (2 * UC) + (j // 2) * UC + (j % 2) * FFN, UC)], i)
                for j in (20, 21):
                    load(u0 + j, units[u0 + j])
                with sp.Fori(0, 4) as i:
                    for j, (a, b) in enumerate(FO_K):
                        load(where[sub, "out"] + j, wo[:, a:b, bass.ds(i * UC, UC)], i)

        @block.scalar
        def _(act):
            A = nc.scalar.activation
            def hi(u, i=None, m=0):
                if u >= NU:
                    return
                act.wait_ge(raw_landed[u % RAW], (0 if i is None else i * (4 * m)) + 16 * (u // RAW + 1))
                if u >= SPL:
                    act.wait_ge(unit_done, (0 if i is None else i * m) + u - SPL + 1)
                A(w_hi[:, u % SPL, 0:size[u]], raw[:, u % RAW, 0:size[u]], ACT.Copy).then_inc(hi_split, 1)

            def pre_norm(sub):
                kind = 0 if sub % 2 == 0 else 2
                if sub != POOL_SUB:
                    for k in range(KD):
                        act.wait_ge(x_new, 4 * sub + k // 2 + 1)
                        A(g_hi[:, k, :], xT[:, k, :], ACT.Copy,
                          scale=gains[:, k, 4 * (sub // 2) + kind:4 * (sub // 2) + kind + 1])\
                            .then_inc(g_hi_ready, 1)
                act.wait_ge(x_new, 4 * sub + 4)
                A(sq[:], xT[:], ACT.Square).then_inc(x_squared, 1)
                act.wait_ge(stat, 2 * sub + 1)
                A(std[:], mix[:, 0, 0:T], ACT.Sqrt, bias=eps_rms, scale=1.0 / D).then_inc(std_ready, 1)

            def post_square(sub, p):
                act.wait_ge(acc_read, pair_at[sub, "out"] + p + 1)
                A(sq[:, 2 * p:2 * p + 2, :], y[:, 2 * p:2 * p + 2, :], ACT.Square).then_inc(y_squared, 1)
                act.wait_ge(y_squared, 4 * sub + p + 1)
                for k in (2 * p, 2 * p + 1):
                    kind = 1 if sub % 2 == 0 else 3
                    ins = A(y[:, k, :], y[:, k, :], ACT.Copy,
                            scale=gains[:, k, 4 * (sub // 2) + kind:4 * (sub // 2) + kind + 1])
                ins.then_inc(y_gained, 1)

            def post_std(sub):
                act.wait_ge(stat, 2 * sub + 2)
                A(std[:], mix[:, 0, 0:T], ACT.Sqrt, bias=eps_rms, scale=1.0 / D).then_inc(std_ready, 1)

            act.dma_start(tbase[:], t_base).then_inc(in_tab, 16)
            act.dma_start(y[:, :, :].rearrange("p k t -> p (k t)")[:, 0:2 * D].rearrange("p (c d) -> p c d", c=2),
                          x_prompt[0].rearrange("(c p) d -> p c d", p=P)).then_inc(in_x, 16)
            sqf = sq[:, :, :].rearrange("p k t -> p (k t)")
            act.dma_start(sqf[0:DECB, 0:D], x_sample.rearrange("b s d -> (b s) d")).then_inc(in_x, 16)
            act.dma_start(sqf[0:16, D:2 * D], gains_d.rearrange("l g d -> (l g) d")).then_inc(in_x, 16)
            act.dma_start(sqf[16:17, D:2 * D], scale_pool).then_inc(in_x, 16)
            hi(0)
            hi(1)

            def ret_mixer(sub):
                r = ret_subs.index(sub)
                u0 = where[sub, "in"]
                if r:
                    act.wait_ge(unit_done, u0)
                act.dma_start(tret[:], t_ret).then_inc(tab_ret, 16)

                def st_view(t, n):
                    return t[r, n % 8, n // 8].rearrange("(k p) v -> p k v", p=P)

                def st_load(n):
                    g = 32 * r + n
                    act.dma_start(st_in[:, g % 3], st_view(state_ret, n)).then_inc(st_landed[g % 3], 16)

                def st_move(n):
                    g = 32 * r + n
                    act.wait_ge(st_updated, g + 1)
                    act.dma_start(st_view(ret_s, n), st_out[:, g % 2]).then_inc(st_stored[g % 2], 16)
                    if n + 3 < 32:
                        st_load(n + 3)

                for n in range(3):
                    st_load(n)

                def sample_out(gh, par):
                    act.wait_ge(qs_done, 8 * (gh + 1))
                    A(oT[:, par, :, SEQ:T], mix[:, 0, 0:32].rearrange("p (v b) -> p v b", v=4), ACT.Copy,
                      scale=1.0 / 16).then_inc(os_ready, 1)

                def gn_square(gh):
                    act.wait_ge(gn_cent, gh + 1)
                    A(gsq[:], oT[:, gh % 2], ACT.Square).then_inc(gn_sq, 1)

                def gn_sqrt(gh):
                    act.wait_ge(gn_var, gh + 1)
                    A(gstd[:], mix[:, 0, 0:T], ACT.Sqrt, bias=eps_gn, scale=1.0 / RDV).then_inc(gn_std, 1)

                def ro_split(gh):
                    act.wait_ge(gn_out, gh + 1)
                    h = gh % RH
                    A(ro_hi[:, 4 * h:4 * h + 4, :], oT[:, gh % 2], ACT.Copy).then_inc(ro_hi_ready, 1)

                for h in range(RH):
                    gh, par = RH * r + h, h % 2
                    ub = u0 + 6 * h
                    pb = pair_at[sub, "in"] + 6 * h
                    for s in range(6):
                        if s >= 4:
                            act.wait_ge(acc_read, pb + s + 1)
                            g2 = gT[:, par, 2 * (s - 4):2 * (s - 4) + 2, :]
                            A(g2, g2, ACT.Silu).then_inc(g_silu, 1)
                        if h and s < 4:
                            st_move(8 * (h - 1) + 2 * s)
                        hi(ub + s + 2)
                        if h and s < 4:
                            st_move(8 * (h - 1) + 2 * s + 1)
                        if s == 3:
                            act.wait_ge(tk_done, gh + 1)
                            A(k_row[:], mix[0:DECB, 2, 0:RDK], ACT.Copy).then_inc(krow_ready, 1)
                            if h == 0:
                                act.wait_ge(tab_ret, 16 * (r + 1))
                            A(kz[:], mix[:, 1, :].rearrange("p (c k) -> p c k", c=2), ACT.Copy,
                              scale=zeta[:, h:h + 1]).then_inc(kz_ready, 1)
                        if h and s == 3:
                            sample_out(gh - 1, 1 - par)
                        if s == 4:
                            act.wait_ge(tv_done, gh + 1)
                            A(vrow[:, :, 0:UC], mix[:, 1, :].rearrange("p (c k) -> p c k", c=2), ACT.Copy)
                            A(vrow[:, :, UC:2 * UC], mix[:, 3, :].rearrange("p (c k) -> p c k", c=2), ACT.Copy)
                            A(v_row[:], mix[0:DECB, 2, :], ACT.Copy).then_inc(vrow_ready, 1)
                            if h == 0:
                                act.wait_ge(stack_zeroed, r + 1)
                            act.wait_ge(krow_ready, gh + 1)
                            A(k_stack[0:8, :], k_row[:], ACT.Copy)
                            A(k_stack[32:40, :], k_row[:], ACT.Copy).then_inc(k_stack_hi, 1)
                            act.wait_ge(vrow_ready, gh + 1)
                            A(v_stack[0:8, :], v_row[:], ACT.Copy)
                            A(v_stack[64:72, :], v_row[:], ACT.Copy).then_inc(v_stack_hi, 1)
                            if h:
                                gn_square(gh - 1)
                        if s == 5:
                            if h:
                                gn_sqrt(gh - 1)
                            act.wait_ge(s0_done, gh + 1)
                            if gh:
                                act.wait_ge(s1_stored, 16 * gh)
                            A(S0[:], mix[:, 2:4, :], ACT.Copy).then_inc(s0_ready, 1)
                            if h >= 2:
                                act.wait_ge(ro_lo_ready, gh - 1)
                            for c in range(2):
                                act.wait_ge(o_done, 2 * gh + c + 1)
                                A(oT[:, par, :, c * P:(c + 1) * P],
                                  mix[:, 1 - c, :].rearrange("p (v n) -> p v n", v=4), ACT.Copy).then_inc(o_ready, 1)
                            if h:
                                ro_split(gh - 1)
                            act.wait_ge(s1_ready, gh + 1)
                            act.dma_start(ret_p[r, 0, h].rearrange("(k p) v -> p k v", p=P), S0[:])\
                                .then_inc(s1_stored, 16)
                gh = RH * r + 3
                uo = where[sub, "out"]
                for b in range(DECB):
                    st_move(24 + b)
                    if b % 4 == 3:
                        hi(uo + 2 + b // 4)
                sample_out(gh, 1)
                gn_square(gh)
                gn_sqrt(gh)
                ro_split(gh)
                for p in range(4):
                    if p >= 2:
                        hi(uo + 2 * p + 2)
                    post_square(sub, p)
                    if p < 2:
                        hi(uo + p + 4)
                    elif p == 2:
                        hi(uo + 7)
                act.wait_ge(s1_stored, 16 * RH * (r + 1))
                for j in range(2):
                    act.wait_ge(st_stored[j], 16 * 16 * (r + 1))
                post_std(sub)
                hi(uo + 9)

            def ffn(sub):
                lay = sub // 2
                u0, uo = where[sub, "in"], where[sub, "out"]
                p0 = pair_at[sub, "in"]

                def pair_step(j, i=None):
                    at = 0 if i is None else i
                    act.wait_ge(acc_read, at * 4 + p0 + 2 * j + 1)
                    A(silu_gate[:, j % 2], gate[:, j % 2], ACT.Silu).then_inc(silu_done, 1)
                    hi(u0 + 2 * j + 2, i, 4)
                    act.wait_ge(hid_ready, at * 2 + (KF // 2) * lay + j + 1)
                    t = at * 4 + 2 * j if i is not None else 2 * j
                    dst = h_hi[:, bass.ds(t, 2), :] if i is not None else h_hi[:, 2 * j:2 * j + 2, :]
                    A(dst, hid[:, j % 2], ACT.Copy).then_inc(h_hi_ready, 1)
                    hi(u0 + 2 * j + 3, i, 4)

                with act.Fori(0, 5) as i:
                    pair_step(0, i)
                    pair_step(1, i)
                pair_step(10)
                for p in range(4):
                    for j in range(4):
                        if j == 3:
                            post_square(sub, p)
                        if p < 3 or j < 3:
                            hi(uo + 4 * p + j + 2)
                post_std(sub)
                hi(uo + 17)

            def pool_mixer(sub):
                u0 = where[sub, "out"]
                act.wait_ge(pad_zeroed, 1)
                act.dma_start(tpool[:], t_pool.rearrange("p (g t) -> p g t", g=4)).then_inc(tab_pool, 16)
                act.dma_start(prev[:], state_pool[0].rearrange("b s d -> (b s) d")).then_inc(prev_in, 16)
                act.dma_start(pool_s[0, :, 0:PREV - 1, :], state_pool[0, :, 1:PREV, :]).then_inc(pool_stored, 16)
                for k in range(4):
                    act.wait_ge(xn_turned, k + 1)
                    n = (PREV, PREV, DECB, DECB)[k]
                    A(pout[0:n, k // 2, (k % 2) * 512:(k % 2) * 512 + 512], mix[0:n, k, :], ACT.Copy)\
                        .then_inc(pout_ready, 1)
                act.wait_ge(pout_ready, 4)
                act.dma_start(pool_p[0, 0], pout[0:PREV, 0, :]).then_inc(pool_stored, 16)
                act.dma_start(pool_s[0, :, PREV - 1, :], pout[0:DECB, 1, :]).then_inc(pool_stored, 16)
                for g in range(4):
                    act.wait_ge(z_ready, g + 1)
                    A(g_hi[:, 2 * g:2 * g + 2, :], zf[:, g % 2], ACT.Copy).then_inc(z_hi_ready, 1)
                for p in range(4):
                    if p < 3:
                        hi(u0 + p + 2)
                    post_square(sub, p)
                act.wait_ge(pool_stored, 48)
                post_std(sub)
                hi(u0 + 5)

            def att_mixer(sub):
                u0, p0 = where[sub, "in"], pair_at[sub, "in"]
                act.wait_ge(cache_zeroed, 1)
                act.dma_start(tatt[:], t_att).then_inc(tab_att, 16)

                def caches_in(quad):
                    for kv, buf in ((0, kc), (1, vc)):
                        cols = slice(quad * UC, (quad + 1) * UC)

                        def view(c):
                            return c[0].rearrange("b w t h e -> w b t (h e)")[:, :, kv, cols]
                        act.dma_start(buf[:, :, 0, :], view(cache0)).then_inc(cache_in, 16)
                        v1 = cache1[0].rearrange("b (w s) t h e -> w b s t (h e)", s=4)[:, :, 0, kv, cols]
                        act.dma_start(buf[0:64, :, 1, :], v1).then_inc(cache_in, 16)
                        v2 = cache2[0].rearrange("b (w s) t h e -> w b s t (h e)", s=16)[:, :, 0, kv, cols]
                        act.dma_start(buf[64:80, :, 1, :], v2).then_inc(cache_in, 16)

                caches_in(0)
                krows = [0]

                def row_out(n):
                    quad, g, kv = n // 6, n // 2 % 3, n % 2
                    par = quad % 2
                    act.wait_ge(row_turned, n + 1)
                    dst = avrow[:, par, g] if kv else akrow
                    if kv == 0 and krows[0]:
                        act.wait_ge(kv_stored, 16 * krows[0])
                    if quad >= 2 and n % 6 == 0:
                        act.wait_ge(row_stored[par], 16 * 3 * (quad // 2))
                        act.wait_ge(srow_stored[par], 16 * 6 * (quad // 2))
                        act.wait_ge(new_in[par], 16 * 6 * (quad // 2))
                    A(dst, mix[:, 2, :].rearrange("p (c k) -> p c k", c=2), ACT.Copy)
                    A(srow[:, par, g, kv, :], mix[0:DECB, 3, 0:UC], ACT.Copy).then_inc(row_evac, 1)
                    act.wait_ge(row_evac, n + 1)
                    cols = slice(quad * UC, (quad + 1) * UC)
                    out = kv_p[g][0, 0].rearrange("w t h e -> w t (h e)")[:, kv, cols]
                    if g == 0:
                        src = dst[:, 1, :]
                    else:
                        out, src = out.rearrange("(c p) n -> p c n", p=P), dst
                    act.dma_start(out, src).then_inc(row_stored[par] if kv else kv_stored, 16)
                    if kv == 0:
                        krows[0] += 1
                    sout = kv_s[g][0, :, 0].rearrange("b t h e -> b t (h e)")[:, kv, cols]
                    act.dma_start(sout, srow[:, par, g, kv, :]).then_inc(srow_stored[par], 16)

                def exps(i):
                    c = i % 2
                    n = 3 * P * (c + 1)
                    act.wait_ge(max_ready, i + 1)
                    A(sc[:, i % 2, 0:n], sc[:, i % 2, 0:n], ACT.Exp, bias=nmax[:, i % 2:i % 2 + 1],
                      accum_out=lsum[:, i % 2:i % 2 + 1]).then_inc(p_exp, 1)
                    act.wait_ge(rl_ready, i + 1)
                    A(sc[:, i % 2, 0:n], sc[:, i % 2, 0:n], ACT.Copy, scale=rl[:, i % 2:i % 2 + 1])\
                        .then_inc(p_ready, 1)

                def turned_out(i):
                    n = 3 * P * (i % 2 + 1)
                    act.wait_ge(pt_done, i + 1)
                    A(pT[:, 0:n], mix[:, 0:2, :].rearrange("p b n -> p (b n)")[:, 0:n], ACT.Copy)\
                        .then_inc(pt_ready, 1)

                def decode(quad):
                    act.wait_ge(dmax_ready, quad + 1)
                    A(dP[:], mix[0:32, 2, 0:227], ACT.Exp, bias=dst[:, 0:1], accum_out=dst[:, 1:2])\
                        .then_inc(dp_exp, 1)

                def new_rows(quad):
                    act.wait_ge(row_evac, 6 * (quad + 1))
                    for g in range(3):
                        for kv, buf in ((0, kc), (1, vc)):
                            act.dma_start(buf[96 + g:97 + g, :, 1, :], srow[:, quad % 2, g, kv, :])\
                                .then_inc(new_in[quad % 2], 16)

                for quad in range(5):
                    for s in range(9):
                        if quad == 4 and s > 8:
                            break
                        n = 9 * quad + s
                        if quad < 4:
                            hi(u0 + n + 2)
                        prev_slot = n - 1
                        if 0 <= prev_slot < 36 and prev_slot % 3:
                            row_out(2 * (prev_slot // 3) + prev_slot % 3 - 1)
                        if quad and s == 0:
                            new_rows(quad - 1)
                        if quad:
                            if 1 <= s:
                                turned_out(8 * (quad - 1) + s - 1)
                            if s < 8:
                                exps(8 * (quad - 1) + s)
                            else:
                                decode(quad - 1)
                                if quad < 4:
                                    act.wait_ge(dpv_read, quad)
                                    caches_in(quad)
                act.wait_ge(kv_stored, 16 * 12)
                for k in range(KD):
                    if k == 0:
                        act.wait_ge(pv_read, 32)
                        act.wait_ge(dpv_read, 4)
                    A(g_hi[:, k, :], y[:, k, :], ACT.Copy).then_inc(ao_hi_ready, 1)
                uo = where[sub, "out"]
                for p in range(4):
                    if p < 3:
                        hi(uo + p + 2)
                    post_square(sub, p)
                for par in range(2):
                    act.wait_ge(row_stored[par], 16 * 6)
                    act.wait_ge(srow_stored[par], 16 * 12)
                post_std(sub)
                hi(uo + 5)

            for sub in range(N_SUB):
                pre_norm(sub)
                if sub % 2:
                    ffn(sub)
                elif sub == POOL_SUB:
                    pool_mixer(sub)
                elif sub == ATT_SUB:
                    att_mixer(sub)
                else:
                    ret_mixer(sub)
            for j in range(6):
                act.wait_ge(fin_turned, j + 1)
                half = slice((j % 2) * 512, (j % 2) * 512 + 512)
                if j < 4:
                    A(rows_out[:, j // 2, half], mix[:, j, :], ACT.Copy).then_inc(fin_ready, 1)
                else:
                    A(srows_out[:, half], acc[0:DECB, j - 4, :], ACT.Copy).then_inc(fin_ready, 1)
            act.wait_ge(fin_ready, 6)
            act.dma_start(y_prompt[0].rearrange("(c p) d -> p c d", p=P), rows_out[:]).then_inc(stored, 16)
            act.dma_start(y_sample.rearrange("b s d -> (b s) d"), srows_out[:]).then_inc(stored, 16)
            act.wait_ge(stored, 32)

        @block.vector
        def _(dve):
            TT, TS, STT = nc.vector.tensor_tensor, nc.vector.tensor_scalar, nc.vector.scalar_tensor_tensor
            steps = [0]

            def mark(ins):
                steps[0] += 1
                ins.then_inc(dve_step, 1)
                return steps[0]

            def link(ins):
                dve.wait_ge(dve_step, mark(ins))

            def wide(ap, n):
                return ap.unsqueeze(1).broadcast_to([ap.shape[0], n, ap.shape[-1]])

            def lo(u, i=None, m=0):
                if u % 2 or u >= NU:
                    return
                dve.wait_ge(hi_split, (0 if i is None else i * m) + u + 1)
                TT(w_lo[:, u % SPL, 0:size[u]], raw[:, u % RAW, 0:size[u]],
                   w_hi[:, u % SPL, 0:size[u]].bitcast(F32), ALU.subtract).then_inc(lo_even, 1)

            def pair_bank(pair):
                return acc[:, 2 * (pair % 2):2 * (pair % 2) + 2, 0:T]

            def rest(sub):
                kind = 0 if sub % 2 == 0 else 2
                if sub != POOL_SUB:
                    for k in range(KD):
                        dve.wait_ge(g_hi_ready, gbase(sub) + k + 1)
                        STT(g_lo[:, k, :], xT[:, k, :],
                            gains[:, k, 4 * (sub // 2) + kind:4 * (sub // 2) + kind + 1],
                            g_hi[:, k, :].bitcast(F32), ALU.mult, ALU.subtract).then_inc(g_lo_ready, 1)
                dve.wait_ge(x_squared, sub + 1)
                link(TT(sq[:, 0:4, :], sq[:, 0:4, :], sq[:, 4:8, :], ALU.add))
                TT(sq[:, 0:2, :], sq[:, 0:2, :], sq[:, 2:4, :], ALU.add).then_inc(pre_summed, 1)
                dve.wait_ge(std_ready, 2 * sub + 1)
                link(nc.vector.reciprocal(rstd_pre[:], std[:]))

            def post_evac(sub, p, u):
                if p == 3:
                    dve.wait_ge(y_squared, 4 * sub + 3)
                    TT(sq[:, 0:2, :], sq[:, 0:2, :], sq[:, 4:6, :], ALU.add).then_inc(post_summed, 1)
                pair = pair_at[sub, "out"] + p
                dve.wait_ge(unit_done, u + 1)
                if sub == POOL_SUB:
                    TS(y[:, 2 * p, :], acc[:, 2 * (pair % 2), 0:T], gains[:, 2 * p, 16:17], None, ALU.mult)
                    TS(y[:, 2 * p + 1, :], acc[:, 2 * (pair % 2) + 1, 0:T], gains[:, 2 * p + 1, 16:17], None,
                       ALU.mult).then_inc(acc_read, 1)
                else:
                    nc.vector.tensor_copy(y[:, 2 * p:2 * p + 2, :], pair_bank(pair)).then_inc(acc_read, 1)
                if p == 1 or p == 2:
                    dve.wait_ge(y_squared, 4 * sub + 2)
                if p == 2:
                    link(TT(sq[:, 0:2, :], sq[:, 0:2, :], sq[:, 2:4, :], ALU.add))

            def post_update(sub):
                dve.wait_ge(std_ready, 2 * sub + 2)
                link(nc.vector.reciprocal(rstd_post[:], std[:]))
                scaled = {}
                for p in range(5):
                    if p < 4:
                        yp = y[:, 2 * p:2 * p + 2, :]
                        dve.wait_ge(y_gained, 4 * sub + p + 1)
                        scaled[p] = mark(TT(yp, yp, wide(rstd_post[:], 2), ALU.mult))
                    if p:
                        q = slice(2 * p - 2, 2 * p)
                        dve.wait_ge(dve_step, scaled[p - 1])
                        TT(xT[:, q, :], xT[:, q, :], y[:, q, :], ALU.add).then_inc(x_new, 1)
                dve.wait_ge(x_new, 4 * (sub + 2))

            for k in range(KD):
                dve.wait_ge(init_turned, k + 1)
                nc.vector.tensor_copy(gains[:, k, :], mix[:, k % 4, T:T + 17])
                nc.vector.tensor_copy(xT[:, k, :], mix[:, k % 4, 0:T]).then_inc(init_read, 1)
            dve.wait_ge(init_read, KD)
            dve.sem_inc(x_new, 4)
            lo(0)

            def ret_mixer(sub):
                r = ret_subs.index(sub)
                u0 = where[sub, "in"]

                def one_key(n):
                    g, b = 32 * r + n, n % 8
                    if b == 0:
                        dve.wait_ge(k_stack_ready, RH * r + n // 8 + 1)
                    if g >= 2:
                        dve.wait_ge(outer_done, g - 1)
                    TS(k_one[:, g % 2, :], k_stack[:].bitcast(F32), one_b[:, b:b + 1], None, ALU.mult)\
                        .then_inc(k_one_ready, 1)

                def update(n):
                    g = 32 * r + n
                    dve.wait_ge(outer_done, g + 1)
                    dve.wait_ge(st_landed[g % 3], 16 * (g // 3 + 1))
                    if g >= 2:
                        dve.wait_ge(st_stored[g % 2], 16 * (g // 2))
                    STT(st_out[:, g % 2], st_in[:, g % 3], GAMMA[n // 8], mix[:, 2:4, :], ALU.mult, ALU.add)\
                        .then_inc(st_updated, 1)

                def gn_first(gh):
                    o = oT[:, gh % 2]
                    dve.wait_ge(o_ready, 2 * gh + 2)
                    dve.wait_ge(os_ready, gh + 1)
                    TT(gsq[:, 0:2, :], o[:, 0:2, :], o[:, 2:4, :], ALU.add).then_inc(gn_sum, 1)

                def gn_center(gh):
                    o = oT[:, gh % 2]
                    dve.wait_ge(gn_mu, gh + 1)
                    STT(o, wide(mix[:, 0, 0:T], 4), -1.0 / RDV, o, ALU.mult, ALU.add).then_inc(gn_cent, 1)
                    dve.wait_ge(gn_sq, gh + 1)
                    TT(gsq[:, 0:2, :], gsq[:, 0:2, :], gsq[:, 2:4, :], ALU.add).then_inc(gn_sum2, 1)

                def gn_last(gh):
                    o = oT[:, gh % 2]
                    dve.wait_ge(gn_std, gh + 1)
                    link(nc.vector.reciprocal(grstd[:], gstd[:]))
                    link(TT(o, o, wide(grstd[:], 4), ALU.mult))
                    dve.wait_ge(g_silu, 2 * gh + 2)
                    TT(o, o, gT[:, gh % 2], ALU.mult).then_inc(gn_out, 1)

                for h in range(RH):
                    gh, par = RH * r + h, h % 2
                    ub, pb = u0 + 6 * h, pair_at[sub, "in"] + 6 * h
                    for s in range(6):
                        if h and s < 4:
                            n = 8 * (h - 1) + 2 * s
                            if s == 0:
                                one_key(n)
                                one_key(n + 1)
                            update(n)
                            update(n + 1)
                        dst = (rq[:, par], rk[:], rv[:, 0], rv[:, 1], gT[:, par, 0:2, :], gT[:, par, 2:4, :])[s]
                        dve.wait_ge(unit_done, ub + s + 1)
                        TT(dst, pair_bank(pb + s), wide(rstd_pre[:], 2), ALU.mult).then_inc(acc_read, 1)
                        if s == 2:
                            if h == 0:
                                dve.wait_ge(tab_ret, 16 * (r + 1))
                            dve.wait_ge(a_done, gh + 1)
                            TT(q_xi[:], rq[:, par, :, P:2 * P], wide(XI[:, h, :], 2), ALU.mult)
                            TT(scoresT[:], mix[:, 1, 0:2 * P].rearrange("p (c n) -> p c n", c=2),
                               wide(DT[:, h, :], 2), ALU.mult).then_inc(at_ready, 1)
                        if h and s < 3:
                            one_key(n + 2)
                            one_key(n + 3)
                        if s == 4:
                            if h:
                                gn_first(gh - 1)
                            dve.wait_ge(k_stack_hi, gh + 1)
                            TT(k_stack[64:72, :], k_row[:], k_stack[0:8, :].bitcast(F32), ALU.subtract)
                            TT(k_stack[96:104, :], k_row[:], k_stack[0:8, :].bitcast(F32), ALU.subtract)\
                                .then_inc(k_stack_ready, 1)
                            dve.wait_ge(v_stack_hi, gh + 1)
                            TT(v_stack[32:40, :], v_row[:], v_stack[0:8, :].bitcast(F32), ALU.subtract)
                            TT(v_stack[96:104, :], v_row[:], v_stack[0:8, :].bitcast(F32), ALU.subtract)\
                                .then_inc(v_stack_ready, 1)
                            if h:
                                gn_center(gh - 1)
                        if s == 5:
                            if h:
                                gn_last(gh - 1)
                            dve.wait_ge(s1_done, gh + 1)
                            STT(S0[:], S0[:], GAMMA[h] ** P, mix[:, 2:4, :], ALU.mult, ALU.add)\
                                .then_inc(s1_ready, 1)
                gh = RH * r + 3
                one_key(24)
                for b in range(DECB):
                    if b < 7:
                        one_key(25 + b)
                    update(24 + b)
                gn_first(gh)
                gn_center(gh)
                gn_last(gh)
                uo = where[sub, "out"]
                for p in range(4):
                    post_evac(sub, p, uo + (2, 3, 5, 7)[p])

            def ffn(sub):
                lay = sub // 2
                u0, uo, p0 = where[sub, "in"], where[sub, "out"], pair_at[sub, "in"]

                def pair_step(j, i=None):
                    at = 0 if i is None else i
                    dve.wait_ge(unit_done, at * 4 + u0 + 2 * j + 1)
                    TT(gate[:, j % 2], pair_bank(p0 + 2 * j), wide(rstd_pre[:], 2), ALU.mult).then_inc(acc_read, 1)
                    lo(u0 + 2 * j + 2, i, 4)
                    dve.wait_ge(unit_done, at * 4 + u0 + 2 * j + 2)
                    n = (KF // 2) * lay + j
                    if n or i is not None:
                        dve.wait_ge(hid_ready, at * 2 + n)
                    TT(up[:], pair_bank(p0 + 2 * j + 1), wide(rstd_pre[:], 2), ALU.mult).then_inc(acc_read, 1)
                    dve.wait_ge(acc_read, at * 4 + p0 + 2 * j + 2)
                    dve.wait_ge(silu_done, at * 2 + n + 1)
                    if n >= 2 or i is not None:
                        dve.wait_ge(h_lo_ready, at * 2 + n - 1)
                    TT(hid[:, j % 2], up[:], silu_gate[:, j % 2], ALU.mult).then_inc(hid_ready, 1)

                pair_step(0)
                pair_step(1)
                with dve.Fori(1, 5) as i:
                    pair_step(0, i)
                    pair_step(1, i)
                pair_step(10)
                for p in range(4):
                    for j in range(4):
                        if j == 3:
                            post_evac(sub, p, uo + 4 * p + 3)
                        else:
                            lo(uo + 4 * p + j + 2)

            def pool_mixer(sub):
                u0 = where[sub, "out"]
                for k in range(KD):
                    ins = STT(xn[:, k, :], xT[:, k, :], gains[:, k, 4 * (sub // 2):4 * (sub // 2) + 1],
                              rstd_pre[:], ALU.mult, ALU.mult)
                ins.then_inc(xn_ready, 1)
                dve.wait_ge(prev_turned, 1)
                n = DECB * PREV
                link(nc.vector.tensor_copy(prevT[:].rearrange("p (b k) n -> p b (k n)", b=2), mix[:, 1:3, 0:4 * n]))
                dve.sem_inc(prevT_ready, 1)
                dve.wait_ge(xn_ready, 1)
                dve.wait_ge(pad_zeroed, 1)
                dve.wait_ge(tab_pool, 16)
                for g, w in enumerate(WINDOWS):
                    pair = xn[:, 2 * g:2 * g + 2, :]
                    link(nc.vector.tensor_copy(pad[:, 0, :, 16:], pair[:, :, 0:SEQ]))
                    for lev in range(g + 1):
                        sh, src, dst = 2 ** lev, pad[:, lev % 2], pad[:, 1 - lev % 2, :, 16:]
                        if lev == g:
                            dst = wsum[:, :, 0:SEQ]
                        link(TT(dst, src[:, :, 16:], src[:, :, 16 - sh:16 + SEQ - sh], ALU.add))
                    back = prevT[:, 2 * g:2 * g + 2, :].rearrange("p k (b s) -> p k b s", b=DECB)
                    link(nc.vector.tensor_reduce(wsum[:, :, SEQ:T], back[:, :, :, PREV + 1 - w:PREV], AX.X, ALU.add))
                    link(TT(wsum[:, :, SEQ:T], wsum[:, :, SEQ:T], pair[:, :, SEQ:T], ALU.add))
                    link(TT(wsum[:], wsum[:], wide(tpool[:, g, :], 2), ALU.mult))
                    if g >= 2:
                        dve.wait_ge(z_lo_ready, g - 1)
                    TT(zf[:, g % 2], wsum[:], pair, ALU.subtract).then_inc(z_ready, 1)
                for p in range(4):
                    if p % 2 == 0:
                        lo(u0 + p + 2)
                    post_evac(sub, p, u0 + p)

            def att_mixer(sub):
                u0, p0 = where[sub, "in"], pair_at[sub, "in"]
                s_first = slopes()[0]

                def pv_evac(i):
                    quad, hh, c = i // 8, i % 8 // 2, i % 2
                    a = 64 * (hh % 2)
                    dve.wait_ge(pv_done, i + 1)
                    nc.vector.tensor_copy(y[a:a + 64, 2 * quad + hh // 2, c * P:(c + 1) * P],
                                          mix[a:a + 64, 1, 2 * P:3 * P]).then_inc(pv_read, 1)

                def scores(i):
                    quad, hh, c = i // 8, i % 8 // 2, i % 2
                    n = 3 * P * (c + 1)
                    if i == 0:
                        dve.wait_ge(tab_att, 16)
                    dve.wait_ge(sc_done, i + 1)
                    STT(sc[:, i % 2, 0:n], TB[c], -float(s_first[4 * quad + hh]),
                        mix[:, 2:4, :].rearrange("p b n -> p (b n)")[:, 0:n], ALU.mult, ALU.add)\
                        .then_inc(sc_biased, 1)
                    dve.wait_ge(sc_biased, i + 1)
                    nc.vector.tensor_reduce(nmax[:, i % 2:i % 2 + 1], sc[:, i % 2, 0:n], AX.X, ALU.max,
                                            negate=True).then_inc(max_ready, 1)
                    dve.wait_ge(p_exp, i + 1)
                    nc.vector.reciprocal(rl[:, i % 2:i % 2 + 1], lsum[:, i % 2:i % 2 + 1]).then_inc(rl_ready, 1)

                def decode(q):
                    dve.wait_ge(cache_in, 16 * 6 * (q + 1))
                    dve.wait_ge(new_in[q % 2], 16 * 6 * (q // 2 + 1))
                    for b in range(DECB):
                        dve.wait_ge(qb_done, 8 * q + b + 1)
                        TT(dprod[:, 0, :], kc[:, b, 0, :], mix[:, 2 + b % 2, 0:UC], ALU.mult)
                        TT(dprod[0:99, 1, :], kc[0:99, b, 1, :], mix[0:99, 2 + b % 2, UC:2 * UC], ALU.mult)\
                            .then_inc(qb_read, 1)
                        dve.wait_ge(qb_read, 8 * q + b + 1)
                        nc.vector.tensor_reduce(dS[:, 0, b, :], dprod[:, 0, :].rearrange("p (h e) -> p h e", h=4),
                                                AX.X, ALU.add)
                        ins = nc.vector.tensor_reduce(dS[0:99, 1, b, :],
                                                      dprod[0:99, 1, :].rearrange("p (h e) -> p h e", h=4),
                                                      AX.X, ALU.add)
                        link(ins)
                    TT(dS[:, 0], dS[:, 0], wide(dbias[:, 0, 4 * q:4 * q + 4], DECB), ALU.add)
                    TT(dS[0:99, 1], dS[0:99, 1], wide(dbias[0:99, 1, 4 * q:4 * q + 4], DECB), ALU.add)\
                        .then_inc(ds_ready, 1)
                    dve.wait_ge(ds_turned, q + 1)
                    nc.vector.tensor_reduce(dst[:, 0:1], mix[0:32, 2, 0:227], AX.X, ALU.max, negate=True)\
                        .then_inc(dmax_ready, 1)
                    dve.wait_ge(dp_exp, q + 1)
                    link(nc.vector.reciprocal(dst[:, 2:3], dst[:, 1:2]))
                    TS(dP[:], dP[:], dst[:, 2:3], None, ALU.mult).then_inc(dp_ready, 1)
                    dve.wait_ge(dpt_done, q + 1)
                    nc.vector.tensor_copy(dPT[:, 0, :], mix[:, 3, 0:32])
                    nc.vector.tensor_copy(dPT[0:99, 1, :], mix[0:99, 3, 32:64]).then_inc(dpt_ready, 1)
                    dve.wait_ge(dpv_done, q + 1)
                    for t in range(2):
                        for half in range(2):
                            a = 64 * half
                            src = mix[a:a + 64, 2, 32 * t:32 * t + 32].rearrange("p (b h) -> p b h", h=4)
                            ins = nc.vector.tensor_copy(y[a:a + 64, 2 * q + t, SEQ:T], src[:, :, 2 * t + half])
                    ins.then_inc(dpv_read, 1)

                for quad in range(5):
                    for s in range(9):
                        n = 9 * quad + s
                        if quad < 4:
                            par, g, kind = quad % 2, s // 3, s % 3
                            dve.wait_ge(unit_done, u0 + n + 1)
                            if kind == 0:
                                STT(aq[:, par, g], pair_bank(p0 + n), ADH ** -0.5, wide(rstd_pre[:], 2),
                                    ALU.mult, ALU.mult).then_inc(acc_read, 1)
                            else:
                                TT(ak[:, par, g] if kind == 1 else av, pair_bank(p0 + n),
                                   wide(rstd_pre[:], 2), ALU.mult).then_inc(acc_read, 1)
                        if quad:
                            a = 8 * (quad - 1) + s
                            if s >= 2:
                                pv_evac(a - 2)
                            if s == 0 and quad >= 2:
                                pv_evac(a - 1)
                            if s < 8:
                                scores(a)
                        if quad < 4:
                            lo(u0 + n + 2)
                        if quad and s == 8:
                            decode(quad - 1)
                pv_evac(31)
                for k in range(KD):
                    dve.wait_ge(ao_hi_ready, k + 1)
                    TT(g_lo[:, k, :], y[:, k, :], g_hi[:, k, :].bitcast(F32), ALU.subtract).then_inc(ao_lo_ready, 1)
                uo = where[sub, "out"]
                for p in range(4):
                    if p % 2 == 0:
                        lo(uo + p + 2)
                    post_evac(sub, p, uo + p)

            for sub in range(N_SUB):
                rest(sub)
                if sub % 2:
                    ffn(sub)
                elif sub == POOL_SUB:
                    pool_mixer(sub)
                elif sub == ATT_SUB:
                    att_mixer(sub)
                else:
                    ret_mixer(sub)
                post_update(sub)

        @block.gpsimd
        def _(pool):
            TT = nc.gpsimd.tensor_tensor

            def lo(u, i=None, m=0, both=False):
                if (u % 2 == 0 and not both) or u >= NU:
                    return
                pool.wait_ge(hi_split, (0 if i is None else i * m) + u + 1)
                TT(w_lo[:, u % SPL, 0:size[u]], raw[:, u % RAW, 0:size[u]],
                   w_hi[:, u % SPL, 0:size[u]].bitcast(F32), ALU.subtract).then_inc(lo_odd if u % 2 else lo_even, 1)

            def ret_mixer(sub):
                r = ret_subs.index(sub)
                u0 = where[sub, "in"]
                if r:
                    pool.wait_ge(unit_done, u0)
                nc.gpsimd.memset(k_stack[:].bitcast(F32), 0.0)
                nc.gpsimd.memset(v_stack[:].bitcast(F32), 0.0).then_inc(stack_zeroed, 1)

                def ro_lo_part(gh):
                    h = gh % RH
                    pool.wait_ge(ro_hi_ready, gh + 1)
                    TT(ro_lo[:, 4 * h:4 * h + 4, :], oT[:, gh % 2], ro_hi[:, 4 * h:4 * h + 4, :].bitcast(F32),
                       ALU.subtract).then_inc(ro_lo_ready, 1)

                for h in range(RH):
                    for s in range(6):
                        lo(u0 + 6 * h + s + 2, both=True)
                        if h and s == 5:
                            ro_lo_part(RH * r + h - 1)
                for j in range(8):
                    lo(where[sub, "out"] + j + 2, both=True)
                    if j == 1:
                        ro_lo_part(RH * r + 3)

            def ffn(sub):
                lay = sub // 2
                u0 = where[sub, "in"]

                def pair_step(j, i=None):
                    at = 0 if i is None else i
                    pool.wait_ge(h_hi_ready, at * 2 + (KF // 2) * lay + j + 1)
                    t = at * 4 + 2 * j
                    cols = slice(t, t + 2) if i is None else bass.ds(t, 2)
                    TT(h_lo[:, cols, :], hid[:, j % 2], h_hi[:, cols, :].bitcast(F32), ALU.subtract)\
                        .then_inc(h_lo_ready, 1)
                    lo(u0 + 2 * j + 3, i, 4)

                with pool.Fori(0, 5) as i:
                    pair_step(0, i)
                    pair_step(1, i)
                pair_step(10)
                for j in range(16):
                    lo(where[sub, "out"] + j + 2)

            lo(1)
            for sub in range(N_SUB):
                if sub % 2:
                    ffn(sub)
                elif sub == POOL_SUB:
                    pool.wait_ge(unit_done, where[sub, "in"])
                    nc.gpsimd.memset(pad[:], 0.0).then_inc(pad_zeroed, 1)
                    for g in range(4):
                        pool.wait_ge(z_hi_ready, g + 1)
                        TT(g_lo[:, 2 * g:2 * g + 2, :], zf[:, g % 2], g_hi[:, 2 * g:2 * g + 2, :].bitcast(F32),
                           ALU.subtract).then_inc(z_lo_ready, 1)
                    for p in range(4):
                        lo(where[sub, "out"] + p + 2)
                elif sub == ATT_SUB:
                    pool.wait_ge(lo_odd, where[sub, "in"] // 2 + 1)
                    pool.wait_ge(unit_done, where[sub, "in"])
                    nc.gpsimd.memset(kc[64:96, :, 1, :], 0.0)
                    nc.gpsimd.memset(vc[64:96, :, 1, :], 0.0).then_inc(cache_zeroed, 1)
                    pool.wait_ge(cache_zeroed, 1)
                    for n in range(36):
                        lo(where[sub, "in"] + n + 2)
                    for p in range(4):
                        lo(where[sub, "out"] + p + 2)
                else:
                    ret_mixer(sub)

        @block.tensor
        def _(pe):
            MM, TR = nc.tensor.matmul, nc.tensor.transpose

            def proj(u, pair, x_hi, x_lo, ks, first=True, last=True, i=None, mu=0, mp=0, ready=None, at=0,
                     done=True, between=()):
                between = dict(enumerate(between))

                def part_over(j, k):
                    if k == len(ks) - 1 and ready is None and between.get(j):
                        between[j]()

                au, ap = (0, 0) if i is None else (i * mu, i * mp)
                pe.wait_ge(hi_split, au + u + 1)
                if first and (i is not None or pair >= 2):
                    pe.wait_ge(acc_read, ap + pair - 1)
                order = [(t, k) for t in range(2) for k in range(len(ks))]
                if ready is not None:
                    order = [(t, k) for k in range(len(ks)) for t in range(2)]
                for t, k in order:
                    if ready is not None and t == 0:
                        ready(ks[k])
                    o = (at + k) * UC + t * P
                    out, wh = acc[:, 2 * (pair % 2) + t, 0:T], w_hi[:, u % SPL, o:o + P]
                    MM(out, wh, x_hi[:, ks[k], :], start=first and k == 0, stop=False)
                    MM(out, wh, x_lo[:, ks[k], :], start=False, stop=False)
                    part_over(t, k)
                pe.wait_ge(lo_even if u % 2 == 0 else lo_odd,
                           (0 if i is None else i * (mu // 2)) + u // 2 + 1)
                for t, k in order:
                    o = (at + k) * UC + t * P
                    ins = MM(acc[:, 2 * (pair % 2) + t, 0:T], w_lo[:, u % SPL, o:o + P], x_hi[:, ks[k], :],
                             start=False, stop=last and k == len(ks) - 1)
                    if t == 0:
                        part_over(2, k)
                if done:
                    ins.then_inc(unit_done, 1)

            def g_ready(sub):
                def wait(k):
                    pe.wait_ge(g_lo_ready, gbase(sub) + k + 1)
                return wait

            def column_sums(parts, signal):
                for j, (src, wait) in enumerate(parts):
                    if wait:
                        pe.wait_ge(*wait)
                    ins = MM(mix[:, 0, 0:T], ones, src, start=(j == 0), stop=(j == len(parts) - 1))
                ins.then_inc(signal, 1)

            def pre_stat(sub):
                column_sums([(sq[:, 0, :], (pre_summed, sub + 1)), (sq[:, 1, :], None)], stat)

            def post_stat(sub):
                column_sums([(sq[:, 0, :], (post_summed, sub + 1)), (sq[:, 1, :], None),
                             (sq[:, 6, :], (y_squared, 4 * sub + 4)), (sq[:, 7, :], None)], stat)

            KK = list(range(KD))

            yf = y[:, :, :].rearrange("p k t -> p (k t)")
            sqf = sq[:, :, :].rearrange("p k t -> p (k t)")
            pe.wait_ge(in_tab, 16)
            pe.wait_ge(in_x, 64)
            for k in range(KD):
                if k >= 4:
                    pe.wait_ge(init_read, k - 3)
                for c in range(2):
                    TR(mix[:, k % 4, c * P:(c + 1) * P], yf[:, c * D + k * P:c * D + (k + 1) * P], ident)
                TR(mix[:, k % 4, SEQ:T], sqf[0:DECB, k * P:(k + 1) * P], ident[0:DECB, 0:DECB])
                TR(mix[:, k % 4, T:T + 17], sqf[0:17, D + k * P:D + (k + 1) * P], ident[0:17, 0:17])\
                    .then_inc(init_turned, 1)

            def ret_mixer(sub):
                r = ret_subs.index(sub)
                u0 = where[sub, "in"]

                def outer(n):
                    g, gh = 32 * r + n, RH * r + n // 8
                    if n % 8 == 0:
                        pe.wait_ge(v_stack_ready, gh + 1)
                        pe.wait_ge(s1_ready, gh + 1)
                        pe.wait_ge(o_ready, 2 * gh + 2)
                    pe.wait_ge(k_one_ready, g + 1)
                    if g:
                        pe.wait_ge(st_updated, g)
                    for kt in range(2):
                        ins = MM(mix[:, 2 + kt, :], k_one[:, g % 2, kt * P:(kt + 1) * P], v_stack[:],
                                 start=True, stop=True)
                    ins.then_inc(outer_done, 1)

                def query(n):
                    g, b = 32 * r + n, n % 8
                    pe.wait_ge(st_updated, g + 1)
                    for vt in range(4):
                        for kt in range(2):
                            ins = MM(mix[:, 0, vt * 8 + b:vt * 8 + b + 1],
                                     st_out[:, g % 2, kt, vt * P:(vt + 1) * P],
                                     rq[:, (n // 8) % 2, kt, SEQ + b:SEQ + b + 1], start=(kt == 0), stop=(kt == 1))
                    ins.then_inc(qs_done, 1)

                def sample(n):
                    if n % 8:
                        query(n - 1)
                    outer(n)

                def gn_mean(gh):
                    pe.wait_ge(os_ready, gh + 1)
                    column_sums([(gsq[:, 0, :], (gn_sum, gh + 1)), (gsq[:, 1, :], None)], gn_mu)

                def gn_variance(gh):
                    pe.wait_ge(gn_cent, gh + 1)
                    column_sums([(gsq[:, 0, :], (gn_sum2, gh + 1)), (gsq[:, 1, :], None)], gn_var)

                for h in range(RH):
                    gh, par = RH * r + h, h % 2
                    ub, pb = u0 + 6 * h, pair_at[sub, "in"] + 6 * h
                    for s in range(6):
                        n = 8 * (h - 1) + 2 * s
                        samples = (lambda: sample(n), None, lambda: sample(n + 1)) if h and s < 4 else ()
                        proj(ub + s, pb + s, g_hi, g_lo, KK,
                             ready=g_ready(sub) if h == 0 and s == 0 else None, between=samples)
                        if h == 0 and s == 0:
                            pre_stat(sub)
                        if s == 2:
                            pe.wait_ge(acc_read, pb + 2)
                            if gh:
                                pe.wait_ge(o_ready, 2 * gh)
                            for c in range(2):
                                for kt in range(2):
                                    ins = MM(mix[:, 1, c * P:(c + 1) * P], rk[:, kt, c * P:(c + 1) * P],
                                             rq[:, par, kt, c * P:(c + 1) * P], start=(kt == 0), stop=(kt == 1))
                            ins.then_inc(a_done, 1)
                        if s == 3:
                            pe.wait_ge(at_ready, gh + 1)
                            for kt in range(2):
                                for c in range(2):
                                    TR(mix[:, 1, c * UC + kt * P:c * UC + (kt + 1) * P],
                                       rk[:, kt, c * P:(c + 1) * P], ident)
                            if h:
                                query(n + 1)
                            for kt in range(2):
                                ins = TR(mix[0:DECB, 2, kt * P:(kt + 1) * P], rk[:, kt, SEQ:T], ident)
                            ins.then_inc(tk_done, 1)
                        if s == 4:
                            pe.wait_ge(acc_read, pb + 4)
                            pe.wait_ge(kz_ready, gh + 1)
                            if h:
                                pe.wait_ge(st_updated, 32 * r + 8 * h)
                            for j, bank in enumerate((1, 3)):
                                for t in range(2):
                                    for c in range(2):
                                        TR(mix[:, bank, c * UC + t * P:c * UC + (t + 1) * P],
                                           rv[:, j, t, c * P:(c + 1) * P], ident)
                                    ins = TR(mix[0:DECB, 2, j * UC + t * P:j * UC + (t + 1) * P],
                                             rv[:, j, t, SEQ:T], ident)
                            ins.then_inc(tv_done, 1)
                            if h:
                                gn_mean(gh - 1)
                        if s == 5:
                            if h:
                                gn_variance(gh - 1)
                            pe.wait_ge(vrow_ready, gh + 1)
                            for kt in range(2):
                                ins = MM(mix[:, 2 + kt, :], kz[:, 0, kt * P:(kt + 1) * P], vrow[:, 0, :],
                                         start=True, stop=True)
                            ins.then_inc(s0_done, 1)
                            for vt in range(4):
                                ins = MM(mix[:, 1, vt * P:(vt + 1) * P], vrow[:, 0, vt * P:(vt + 1) * P],
                                         scoresT[:, 0, :], start=True, stop=True)
                            ins.then_inc(o_done, 1)
                            pe.wait_ge(s0_ready, gh + 1)
                            for kt in range(2):
                                ins = MM(mix[:, 2 + kt, :], kz[:, 1, kt * P:(kt + 1) * P], vrow[:, 1, :],
                                         start=True, stop=True)
                            if h:
                                pe.wait_ge(gn_std, gh)
                            for vt in range(4):
                                out = mix[:, 0, vt * P:(vt + 1) * P]
                                MM(out, vrow[:, 1, vt * P:(vt + 1) * P], scoresT[:, 1, :], start=True, stop=False)
                                for kt in range(2):
                                    ins = MM(out, S0[:, kt, vt * P:(vt + 1) * P], q_xi[:, kt, :],
                                             start=False, stop=(kt == 1))
                            ins.then_inc(o_done, 1)
                            pe.wait_ge(o_done, 2 * gh + 2)
                            pe.sem_inc(s1_done, 1)
                uo, po = where[sub, "out"], pair_at[sub, "out"]
                first_half, pieces = list(range(8)), (list(range(8, 12)), list(range(12, 16)))
                pe.wait_ge(ro_lo_ready, RH * r + 2)
                for p in range(2):
                    n = 24 + 4 * p
                    proj(uo + p, po + p, ro_hi, ro_lo, first_half, last=False,
                         between=(lambda: sample(n), lambda: sample(n + 1), lambda: sample(n + 2)))
                    sample(n + 3)
                query(31)
                pe.wait_ge(ro_lo_ready, RH * r + 3)
                proj(uo + 2, po, ro_hi, ro_lo, pieces[0], first=False, last=False, done=False)
                gn_mean(RH * r + 3)
                proj(uo + 3, po + 1, ro_hi, ro_lo, pieces[0], first=False, last=False, done=False)
                gn_variance(RH * r + 3)
                pe.wait_ge(ro_lo_ready, RH * r + 4)
                for p in range(2):
                    proj(uo + 2 + p, po + p, ro_hi, ro_lo, pieces[1], first=False, at=4)
                for p in (2, 3):
                    for j in range(2):
                        proj(uo + 2 * p + j, po + p, ro_hi, ro_lo, list(range(8 * j, 8 * j + 8)),
                             first=(j == 0), last=(j == 1))

            def ffn(sub):
                lay = sub // 2
                u0, uo = where[sub, "in"], where[sub, "out"]
                p0, po = pair_at[sub, "in"], pair_at[sub, "out"]
                proj(u0, p0, g_hi, g_lo, KK, ready=g_ready(sub))
                pre_stat(sub)
                proj(u0 + 1, p0 + 1, g_hi, g_lo, KK)
                with pe.Fori(0, 5) as i:
                    for j in range(4):
                        proj(u0 + 2 + j, p0 + 2 + j, g_hi, g_lo, KK, i=i, mu=4, mp=4)
                with pe.Fori(0, 2) as i:
                    for p in range(2):
                        for j, (a, b) in enumerate(FO_K):
                            pe.wait_ge(h_lo_ready, (KF // 2) * lay + (b + 1) // 2)
                            proj(uo + 4 * p + j, po + p, h_hi, h_lo, list(range(a, b)), first=(j == 0),
                                 last=(j == 3), i=i, mu=8, mp=2)

            def pool_mixer(sub):
                pre_stat(sub)
                pe.wait_ge(prev_in, 16)
                n = DECB * PREV
                for k in range(KD):
                    ins = TR(mix[:, 1 + k // 4, (k % 4) * n:(k % 4 + 1) * n], prev[:, k * P:(k + 1) * P],
                             ident[0:n, 0:n])
                ins.then_inc(prev_turned, 1)
                pe.wait_ge(xn_ready, 1)
                pe.wait_ge(prevT_ready, 1)
                for bank in range(4):
                    for k in range(4):
                        a, b = (SEQ - PREV, SEQ) if bank < 2 else (SEQ, T)
                        ins = TR(mix[0:b - a, bank, k * P:(k + 1) * P], xn[:, 4 * (bank % 2) + k, a:b], ident)
                    ins.then_inc(xn_turned, 1)
                for g in range(4):
                    pe.wait_ge(z_lo_ready, g + 1)
                    proj(where[sub, "out"] + g, pair_at[sub, "out"] + g, g_hi, g_lo, [2 * g, 2 * g + 1])

            def att_mixer(sub):
                u0, p0 = where[sub, "in"], pair_at[sub, "in"]
                turned = [0]

                def turn_rows(m):
                    quad, g, kind = m // 9, m % 9 // 3, m % 3
                    src = ak[:, quad % 2, g] if kind == 1 else av
                    pe.wait_ge(acc_read, p0 + m + 1)
                    if turned[0]:
                        pe.wait_ge(row_evac, turned[0])
                    if quad >= 1 and m % 9 == 1:
                        pass
                    for t in range(2):
                        for c in range(2):
                            TR(mix[:, 2, c * UC + t * P:c * UC + (t + 1) * P], src[:, t, c * P:(c + 1) * P], ident)
                        ins = TR(mix[0:DECB, 3, t * P:(t + 1) * P], src[:, t, SEQ:T], ident)
                    ins.then_inc(row_turned, 1)
                    turned[0] += 1

                def values(i):
                    quad, hh, c = i // 8, i % 8 // 2, i % 2
                    pe.wait_ge(pt_ready, i + 1)
                    if i:
                        pe.wait_ge(pv_read, i)
                    pe.wait_ge(row_evac, 6 * (quad + 1))
                    t = hh // 2
                    blocks = [(g, kb) for g in range(3) for kb in range(c + 1)]
                    for n, (g, kb) in enumerate(blocks):
                        ins = MM(mix[:, 1, 2 * P:3 * P], avrow[:, quad % 2, g, kb, t * P:(t + 1) * P],
                                 pT[:, n * P:(n + 1) * P], start=(n == 0), stop=(n == len(blocks) - 1))
                    ins.then_inc(pv_done, 1)

                def turn_probs(i):
                    n = 3 * (i % 2 + 1)
                    pe.wait_ge(p_ready, i + 1)
                    if i:
                        pe.wait_ge(pt_ready, i)
                    for j in range(n):
                        if j == 4:
                            pe.wait_ge(pv_read, i)
                        ins = TR(mix[:, j // 4, (j % 4) * P:(j % 4 + 1) * P], sc[:, i % 2, j * P:(j + 1) * P], ident)
                    ins.then_inc(pt_done, 1)

                def scores(i):
                    quad, hh, c = i // 8, i % 8 // 2, i % 2
                    a, t = 64 * (hh % 2), hh // 2
                    n = (c + 1) * P
                    if i:
                        pe.wait_ge(sc_biased, i)
                    pe.wait_ge(row_evac, turned[0])
                    for g in range(3):
                        at = g * n
                        ins = MM(mix[:, 2 + at // 512, at % 512:at % 512 + n],
                                 aq[a:a + 64, quad % 2, g, t, c * P:(c + 1) * P],
                                 ak[a:a + 64, quad % 2, g, t, 0:n], start=True, stop=True)
                    ins.then_inc(sc_done, 1)

                def decode(q):
                    par = q % 2
                    pe.wait_ge(sc_biased, 8 * (q + 1))
                    pe.wait_ge(row_evac, turned[0])
                    for b in range(DECB):
                        bank = 2 + b % 2
                        if 8 * q + b - 1 > 0 and b >= 2:
                            pe.wait_ge(qb_read, 8 * q + b - 1)
                        for t in range(2):
                            def query(g):
                                return aq[:, par, g, t, SEQ + b:SEQ + b + 1]
                            MM(mix[:, bank, t * P:(t + 1) * P], query(0).broadcast_to([P, P]), ident,
                               start=True, stop=True)
                            cols = slice(UC + t * P, UC + (t + 1) * P)
                            MM(mix[0:64, bank, cols], query(1).broadcast_to([P, 64]), ident, start=True, stop=True)
                            MM(mix[64:96, bank, cols], query(2).broadcast_to([P, 32]), ident, start=True, stop=True)
                            ins = MM(mix[96:99, bank, cols], aq[:, par, 0:3, t, SEQ + b], ident,
                                     start=True, stop=True)
                        ins.then_inc(qb_done, 1)
                    pe.wait_ge(ds_ready, q + 1)
                    TR(mix[0:32, 2, 0:P], dS[:, 0].rearrange("p b h -> p (b h)"), ident)
                    TR(mix[0:32, 2, P:P + 99], dS[0:99, 1].rearrange("p b h -> p (b h)"), ident[0:99, 0:99])\
                        .then_inc(ds_turned, 1)
                    pe.wait_ge(dp_ready, q + 1)
                    TR(mix[:, 3, 0:32], dP[:, 0:P], ident[0:32, 0:32])
                    TR(mix[0:99, 3, 32:64], dP[:, P:P + 99], ident[0:32, 0:32]).then_inc(dpt_done, 1)
                    pe.wait_ge(dpt_ready, q + 1)
                    for b in range(DECB):
                        for t in range(2):
                            out = mix[:, 2, 32 * t + 4 * b:32 * t + 4 * b + 4]
                            MM(out, vc[:, b, 0, t * P:(t + 1) * P], dPT[:, 0, 4 * b:4 * b + 4],
                               start=True, stop=False)
                            ins = MM(out, vc[0:99, b, 1, t * P:(t + 1) * P], dPT[0:99, 1, 4 * b:4 * b + 4],
                                     start=False, stop=True)
                    ins.then_inc(dpv_done, 1)

                for quad in range(5):
                    for s in range(9):
                        n = 9 * quad + s
                        if quad < 4:
                            proj(u0 + n, p0 + n, g_hi, g_lo, KK, ready=g_ready(sub) if n == 0 else None)
                            if n == 0:
                                pre_stat(sub)
                        if quad >= 2 and s == 0:
                            pe.wait_ge(dpv_read, quad - 1)
                        if 0 <= n - 1 < 36 and (n - 1) % 3:
                            if quad and s > 0:
                                pe.wait_ge(sc_biased, 8 * (quad - 1) + min(s, 8))
                            turn_rows(n - 1)
                        if quad:
                            a = 8 * (quad - 1) + s
                            if s >= 2:
                                values(a - 2)
                            if s == 0 and quad >= 2:
                                values(a - 1)
                            if s >= 1:
                                turn_probs(a - 1)
                            if s < 8:
                                scores(a)
                            else:
                                decode(quad - 1)
                values(31)
                for p in range(4):
                    proj(where[sub, "out"] + p, pair_at[sub, "out"] + p, g_hi, g_lo, KK,
                         ready=(lambda k: pe.wait_ge(ao_lo_ready, k + 1)) if p == 0 else None)

            for sub in range(N_SUB):
                if sub % 2:
                    ffn(sub)
                elif sub == POOL_SUB:
                    pool_mixer(sub)
                elif sub == ATT_SUB:
                    att_mixer(sub)
                else:
                    ret_mixer(sub)
                post_stat(sub)
            pe.wait_ge(x_new, 4 * (N_SUB + 1))
            for j in range(6):
                for k in range(4):
                    kk = 4 * (j % 2) + k
                    if j < 4:
                        ins = TR(mix[:, j, k * P:(k + 1) * P], xT[:, kk, (j // 2) * P:(j // 2 + 1) * P], ident)
                    else:
                        ins = TR(acc[0:DECB, j - 4, k * P:(k + 1) * P], xT[:, kk, SEQ:T], ident)
                ins.then_inc(fin_turned, 1)


_INS = ["x_prompt", "x_sample", "state_ret", "state_pool", "cache_kv_g0", "cache_kv_g1", "cache_kv_g2",
        "norm_gains", "w_in_ret", "w_out_ret", "w_grp_pool", "scale_pool", "w_in_attn", "w_out_attn",
        "w_ffn_in", "w_ffn_out"]
_OUTS = [(1, SEQ, D), (DECB, 1, D), (2, 1, RH, RDK, RDV), (2, DECB, RH, RDK, RDV), (1, 1, PREV, D),
         (1, DECB, PREV, D), (1, 1, 128, 2, AH, ADH), (1, DECB, 1, 2, AH, ADH), (1, 1, 256, 2, AH, ADH),
         (1, DECB, 1, 2, AH, ADH), (1, 1, 256, 2, AH, ADH), (1, DECB, 1, 2, AH, ADH)]


def kernel(**inputs):
    import concourse.bacc as _bacc
    from concourse.bass_utils import run_bass_kernel_spmd as _run

    nc = _bacc.Bacc("TRN2", target_bir_lowering=False, num_devices=1)
    arrays, args = {}, []
    named = [(name, np.ascontiguousarray(inputs[name])) for name in _INS]
    named += list(zip(("t_base", "t_ret", "t_pool", "t_att"), shape_tables()))
    for name, a in named:
        arrays[f"in_{name}_dram"] = a
        args.append(nc.dram_tensor(f"in_{name}_dram", a.shape, mybir.dt.from_np(a.dtype), kind="ExternalInput").ap())
    for i, shape in enumerate(_OUTS):
        args.append(nc.dram_tensor(f"out_{i}_dram", shape, F32, kind="ExternalOutput").ap())
    trunk(nc, args)
    r = _run(nc, [arrays], core_ids=[0])
    return tuple(r.results[0][f"out_{i}_dram"] for i in range(len(_OUTS)))
```
